# Optimizing a Trainium2 kernel written in Bass

```python
import jax, jax.numpy as jnp
from jax import lax
import numpy as np

D_MODEL = 1024
BATCH = 1
SEQ = 128
DEPTH = 2
DEC_BATCH = 1
DEC_SEQ = 128
PAST_LEN = 128

GRID_W = 64
MIX_WIDTH = D_MODEL
HEAD_DIM = 64
ATT_WIDTH = MIX_WIDTH // 2
N_ATT_HEADS = ATT_WIDTH // HEAD_DIM
N_KV_HEADS = N_ATT_HEADS // 4
ML_WIDTH = MIX_WIDTH - ATT_WIDTH
N_ML_HEADS = 4
ML_HEAD_DIM = ML_WIDTH // N_ML_HEADS
MLSTM_CHUNK = 64
Q_BLOCK = 128
ROPE_BASE = 10000.0
N_EXPERTS = 16
N_EXPERT_GROUPS = 4
EXPERTS_PER_GROUP = N_EXPERTS // N_EXPERT_GROUPS
TOP_K = 2
D_EXPERT = 512
EPS = 1e-6
IN_WIDTHS = (ATT_WIDTH, N_KV_HEADS * HEAD_DIM, N_KV_HEADS * HEAD_DIM,
             ML_WIDTH, ML_WIDTH, ML_WIDTH, ML_WIDTH, 2 * N_ML_HEADS, 2 * N_ML_HEADS)
D_IN = sum(IN_WIDTHS)

kernel_name = 'hybrid_mlstm_gqa_grouped_moe_diffusion_step'

def _rmsnorm(x, g):
    x32 = x.astype(jnp.float32)
    y = x32 * lax.rsqrt(jnp.mean(x32 * x32, axis=-1, keepdims=True) + EPS)
    return (y * g.astype(jnp.float32)).astype(x.dtype)

def _modulation(cond, w_mod, b_mod):
    m = (jax.nn.silu(cond) @ w_mod + b_mod)[:, None, :]
    return jnp.split(m, 6, axis=-1)

def _project(h, w_in, b_igate, b_fgate, g_q, g_k):
    B, S, _ = h.shape
    split_points = np.cumsum(IN_WIDTHS)[:-1].tolist()
    aq, ak, av, mq, mk, mv, mo, mi, mf = jnp.split(h @ w_in, split_points, axis=-1)
    aq = _rmsnorm(aq.reshape(B, S, N_ATT_HEADS, HEAD_DIM), g_q)
    ak = _rmsnorm(ak.reshape(B, S, N_KV_HEADS, HEAD_DIM), g_k)
    av = av.reshape(B, S, N_KV_HEADS, HEAD_DIM)
    heads = lambda a: a.reshape(B, S, N_ML_HEADS, ML_HEAD_DIM).transpose(0, 2, 1, 3).astype(jnp.float32)
    mq, mk, mv = heads(mq), heads(mk) * (ML_HEAD_DIM ** -0.5), heads(mv)
    gate = lambda a, b: (a.reshape(B, S, 2, N_ML_HEADS).astype(jnp.float32)
                         + b.astype(jnp.float32)).transpose(2, 0, 3, 1)
    ig = gate(mi, b_igate)
    lf = jax.nn.log_sigmoid(gate(mf, b_fgate))
    og = jax.nn.sigmoid(mo)
    return (aq, ak, av), (mq, mk, mv, ig, lf), og

def _axial_rope(x, row, col):
    half = HEAD_DIM // 2
    freqs = ROPE_BASE ** (-jnp.arange(0, half, 2, dtype=jnp.float32) / half)
    x32 = x.astype(jnp.float32)

    def rot(xh, pos):
        ang = pos.astype(jnp.float32)[:, None] * freqs[None, :]
        cos = jnp.cos(ang)[None, :, None, :]
        sin = jnp.sin(ang)[None, :, None, :]
        x1, x2 = jnp.split(xh, 2, axis=-1)
        return jnp.concatenate([x1 * cos - x2 * sin, x1 * sin + x2 * cos], axis=-1)

    out = jnp.concatenate([rot(x32[..., :half], row), rot(x32[..., half:], col)], axis=-1)
    return out.astype(x.dtype)

def _block_attention(q, k, v):
    B, Sq, H, dh = q.shape
    G = k.shape[2]
    R = H // G
    nb = Sq // Q_BLOCK
    qb = q.reshape(B, nb, Q_BLOCK, G, R, dh).transpose(1, 0, 2, 3, 4, 5)
    scale = dh ** -0.5

    def one_block(qblk):
        s = jnp.einsum('bqgrd,bkgd->bgrqk', qblk, k).astype(jnp.float32) * scale
        p = jax.nn.softmax(s, axis=-1).astype(v.dtype)
        return jnp.einsum('bgrqk,bkgd->bqgrd', p, v)

    o = lax.map(one_block, qb)
    return o.transpose(1, 0, 2, 3, 4, 5).reshape(B, Sq, H * dh)

def _mlstm_chunkwise(q, k, v, ig, lf, C0, n0, m0):
    B, H, S, DK = q.shape
    L = MLSTM_CHUNK
    nc = S // L
    chunks = lambda a: jnp.moveaxis(a.reshape(B, H, nc, L, *a.shape[3:]), 2, 0)
    causal = jnp.tril(jnp.ones((L, L), dtype=bool))

    def step(carry, inp):
        C, n, m = carry
        qb, kb, vb, ib, fb = inp
        b = jnp.cumsum(fb, axis=-1)
        d = b[..., :, None] - b[..., None, :] + ib[..., None, :]
        d = jnp.where(causal, d, -jnp.inf)
        inter = b + m[..., None]
        m_t = jnp.maximum(inter, jnp.max(d, axis=-1))
        w_intra = jnp.exp(d - m_t[..., None])
        w_inter = jnp.exp(inter - m_t)
        s = jnp.einsum('bhtd,bhsd->bhts', qb, kb) * w_intra
        num = (w_inter[..., None] * jnp.einsum('bhtd,bhde->bhte', qb, C)
               + jnp.einsum('bhts,bhse->bhte', s, vb))
        den = w_inter * jnp.einsum('bhtd,bhd->bht', qb, n) + jnp.sum(s, axis=-1)
        h = num / jnp.maximum(jnp.abs(den), jnp.exp(-m_t))[..., None]
        b_last = b[..., -1]
        m_new = m_t[..., -1]
        decay = jnp.exp(b_last + m - m_new)
        w_s = jnp.exp(b_last[..., None] - b + ib - m_new[..., None])
        kw = kb * w_s[..., None]
        C_new = decay[..., None, None] * C + jnp.einsum('bhsd,bhse->bhde', kw, vb)
        n_new = decay[..., None] * n + jnp.sum(kw, axis=2)
        return (C_new, n_new, m_new), h

    fin, hs = lax.scan(step, (C0, n0, m0), (chunks(q), chunks(k), chunks(v), chunks(ig), chunks(lf)))
    h = jnp.moveaxis(hs, 0, 2).reshape(B, H, S, v.shape[-1])
    return h, fin

def _mlstm_bidir(mq, mk, mv, ig, lf, init_f, init_b):
    h_f, fin_f = _mlstm_chunkwise(mq, mk, mv, ig[0], lf[0], *init_f)
    rev = lambda a: jnp.flip(a, axis=2)
    h_b, fin_b = _mlstm_chunkwise(rev(mq), rev(mk), rev(mv), rev(ig[1]), rev(lf[1]), *init_b)
    return h_f + rev(h_b), fin_f, fin_b

def _mixer_out(att, h_ml, og, g_mh, w_out):
    B, S, _ = og.shape
    h = _rmsnorm(h_ml.transpose(0, 2, 1, 3), g_mh.reshape(N_ML_HEADS, ML_HEAD_DIM))
    ml = (og * h.reshape(B, S, ML_WIDTH)).astype(att.dtype)
    return jnp.concatenate([att, ml], axis=-1) @ w_out

def _moe(h, w_router, b_router, w_gate, w_up, w_down):
    B, S, D = h.shape
    xt = h.reshape(B * S, D)
    scores = jax.nn.softmax((xt @ w_router).astype(jnp.float32), axis=-1)
    sel = scores + b_router.astype(jnp.float32)
    grp_score = jnp.sum(lax.top_k(sel.reshape(-1, N_EXPERT_GROUPS, EXPERTS_PER_GROUP), TOP_K)[0], axis=-1)
    grp = jnp.argmax(grp_score, axis=-1)
    in_grp = grp[:, None] == (jnp.arange(N_EXPERTS) // EXPERTS_PER_GROUP)[None, :]
    _, idx = lax.top_k(jnp.where(in_grp, sel, -jnp.inf), TOP_K)
    w = jnp.take_along_axis(scores, idx, axis=-1)
    w = w / jnp.sum(w, axis=-1, keepdims=True)
    gates = jnp.einsum('nk,nke->ne', w, jax.nn.one_hot(idx, N_EXPERTS, dtype=jnp.float32))
    hid = jax.nn.silu(jnp.einsum('nd,edf->nef', xt, w_gate)) * jnp.einsum('nd,edf->nef', xt, w_up)
    hid = hid * gates.astype(hid.dtype)[..., None]
    y = jnp.einsum('nef,efd->nd', hid, w_down)
    return y.reshape(B, S, D)

def setup_inputs(seed: int = 0) -> dict:
    key = jax.random.key(seed)
    ks = jax.random.split(key, 26)
    nrm = lambda k, shape, s=1.0: jax.random.normal(k, shape, jnp.float32) * s
    L = DEPTH
    return {
        'x_prompt': nrm(ks[0], (BATCH, SEQ, D_MODEL)),
        'x_sample': nrm(ks[1], (DEC_BATCH, DEC_SEQ, D_MODEL)),
        'c': nrm(ks[2], (DEC_BATCH, D_MODEL)),
        'cache_k': nrm(ks[3], (DEC_BATCH, L, PAST_LEN, N_KV_HEADS, HEAD_DIM)),
        'cache_v': nrm(ks[4], (DEC_BATCH, L, PAST_LEN, N_KV_HEADS, HEAD_DIM)),
        'state_C': nrm(ks[5], (DEC_BATCH, L, 2, N_ML_HEADS, ML_HEAD_DIM, ML_HEAD_DIM), 0.3),
        'state_n': nrm(ks[6], (DEC_BATCH, L, 2, N_ML_HEADS, ML_HEAD_DIM), 0.3),
        'state_m': nrm(ks[7], (DEC_BATCH, L, 2, N_ML_HEADS), 0.5),
        'c_ctx': nrm(ks[8], (D_MODEL,)),
        'w_mod': nrm(ks[9], (L, D_MODEL, 6 * D_MODEL), 0.5 * D_MODEL ** -0.5),
        'b_mod': nrm(ks[10], (L, 6 * D_MODEL), 0.02),
        'g_mix': 1.0 + nrm(ks[11], (L, D_MODEL), 0.1),
        'g_ffn': 1.0 + nrm(ks[12], (L, D_MODEL), 0.1),
        'w_in': nrm(ks[13], (L, D_MODEL, D_IN), D_MODEL ** -0.5),
        'b_igate': nrm(ks[14], (L, 2, N_ML_HEADS), 0.1),
        'b_fgate': jnp.linspace(3.0, 6.0, N_ML_HEADS, dtype=jnp.float32) + nrm(ks[15], (L, 2, N_ML_HEADS), 0.1),
        'g_q': 1.0 + nrm(ks[16], (L, HEAD_DIM), 0.1),
        'g_k': 1.0 + nrm(ks[17], (L, HEAD_DIM), 0.1),
        'g_mh': 1.0 + nrm(ks[18], (L, ML_WIDTH), 0.1),
        'w_out': nrm(ks[19], (L, MIX_WIDTH, D_MODEL), MIX_WIDTH ** -0.5),
        'w_router': nrm(ks[20], (D_MODEL, N_EXPERTS), D_MODEL ** -0.5),
        'b_router': nrm(ks[21], (N_EXPERTS,), 0.01),
        'w_e_gate': nrm(ks[22], (L, N_EXPERTS, D_MODEL, D_EXPERT), D_MODEL ** -0.5),
        'w_e_up': nrm(ks[23], (L, N_EXPERTS, D_MODEL, D_EXPERT), D_MODEL ** -0.5),
        'w_e_down': nrm(ks[24], (L, N_EXPERTS, D_EXPERT, D_MODEL), D_EXPERT ** -0.5),
    }

def reference(x_prompt, x_sample, c, cache_k, cache_v, state_C, state_n, state_m, c_ctx,
              w_mod, b_mod, g_mix, g_ffn, w_in, b_igate, b_fgate, g_q, g_k, g_mh, w_out,
              w_router, b_router, w_e_gate, w_e_up, w_e_down):
    f32 = jnp.float32

    x = x_prompt
    B = x.shape[0]
    zero = (jnp.zeros((B, N_ML_HEADS, ML_HEAD_DIM, ML_HEAD_DIM), f32),
            jnp.zeros((B, N_ML_HEADS, ML_HEAD_DIM), f32),
            jnp.zeros((B, N_ML_HEADS), f32))
    ks, vs, Cs, ns, ms = [], [], [], [], []
    for l in range(DEPTH):
        sh1, sc1, gt1, sh2, sc2, gt2 = _modulation(c_ctx[None, :], w_mod[l], b_mod[l])
        h = _rmsnorm(x, g_mix[l]) * (1 + sc1) + sh1
        (aq, ak, av), (mq, mk, mv, ig, lf), og = _project(h, w_in[l], b_igate[l], b_fgate[l], g_q[l], g_k[l])
        att = _block_attention(aq, ak, av)
        h_ml, fin_f, fin_b = _mlstm_bidir(mq, mk, mv, ig, lf, zero, zero)
        x = (x + gt1 * _mixer_out(att, h_ml, og, g_mh[l], w_out[l])).astype(x_prompt.dtype)
        h = _rmsnorm(x, g_ffn[l]) * (1 + sc2) + sh2
        x = (x + gt2 * _moe(h, w_router, b_router, w_e_gate[l], w_e_up[l], w_e_down[l])).astype(x_prompt.dtype)
        ks.append(ak)
        vs.append(av)
        Cs.append(jnp.stack([fin_f[0], fin_b[0]], axis=1))
        ns.append(jnp.stack([fin_f[1], fin_b[1]], axis=1))
        ms.append(jnp.stack([fin_f[2], fin_b[2]], axis=1))
    y_prompt = x
    new_cache_k = jnp.stack(ks, axis=1)
    new_cache_v = jnp.stack(vs, axis=1)
    new_state_C = jnp.stack(Cs, axis=1)
    new_state_n = jnp.stack(ns, axis=1)
    new_state_m = jnp.stack(ms, axis=1)

    x = x_sample
    S = x.shape[1]
    n_rows = S // GRID_W
    row = jnp.repeat(jnp.arange(n_rows), GRID_W)
    col = jnp.tile(jnp.arange(GRID_W), n_rows)
    for l in range(DEPTH):
        sh1, sc1, gt1, sh2, sc2, gt2 = _modulation(c, w_mod[l], b_mod[l])
        h = _rmsnorm(x, g_mix[l]) * (1 + sc1) + sh1
        (aq, ak, av), (mq, mk, mv, ig, lf), og = _project(h, w_in[l], b_igate[l], b_fgate[l], g_q[l], g_k[l])
        aq = _axial_rope(aq, row, col)
        ak = _axial_rope(ak, row, col)
        k_all = jnp.concatenate([cache_k[:, l].astype(ak.dtype), ak], axis=1)
        v_all = jnp.concatenate([cache_v[:, l].astype(av.dtype), av], axis=1)
        att = _block_attention(aq, k_all, v_all)
        init_f = (state_C[:, l, 0].astype(f32), state_n[:, l, 0].astype(f32), state_m[:, l, 0].astype(f32))
        init_b = (state_C[:, l, 1].astype(f32), state_n[:, l, 1].astype(f32), state_m[:, l, 1].astype(f32))
        h_ml, _, _ = _mlstm_bidir(mq, mk, mv, ig, lf, init_f, init_b)
        x = (x + gt1 * _mixer_out(att, h_ml, og, g_mh[l], w_out[l])).astype(x_sample.dtype)
        h = _rmsnorm(x, g_ffn[l]) * (1 + sc2) + sh2
        x = (x + gt2 * _moe(h, w_router, b_router, w_e_gate[l], w_e_up[l], w_e_down[l])).astype(x_sample.dtype)
    y_sample = x

    return (y_prompt, y_sample, new_cache_k, new_cache_v, new_state_C, new_state_n, new_state_m)


_drawn_inputs = setup_inputs


def setup_inputs(seed=0):
    import zlib

    import numpy as np

    out = dict(_drawn_inputs(seed))
    spreads = {}
    factors = {'g_q': 5.595, 'state_m': 2.681}
    for name, (base, spread) in spreads.items():
        noise = np.random.default_rng([zlib.crc32(name.encode()), seed]).standard_normal(out[name].shape)
        drawn = base * np.exp(spread * noise) if base else spread * noise
        out[name] = __import__('jax').numpy.asarray(drawn.astype(out[name].dtype))
    for name, factor in factors.items():
        out[name] = (out[name] * factor).astype(out[name].dtype)
    return out
```

```python
from contextlib import ExitStack

import numpy as np

import concourse.bass as bass
from concourse import mybir

F32 = mybir.dt.float32
I32 = mybir.dt.int32
BF16 = mybir.dt.bfloat16
ALU = mybir.AluOpType
ACT = mybir.ActivationFunctionType
AX_X = mybir.AxisListType.X

P = 128
D = 1024
KD = D // P
DEPTH = 2
NB = 2
TOK = NB * P
GRID_W = 64
HD = 64
NQ = 8
NKV = 2
MH = 4
MD = 128
ML = MH * MD
E = 16
GROUPS = 4
F = 512
KF = F // P
EPS = 1e-6
ROPE_BASE = 10000.0
SLOTS = 64
PAIRS = E // 2
MOD = 6 * D
MODC = MOD // P
QW = (NQ + NKV) * HD
GATE0 = 2816
NG = 16
RING = 6
WB = 512
MOD_SLOTS = MOD // WB
ROWS_L = MODC + KD + KD + MH + 8
A_GMIX, A_GFFN, A_GMH, A_N0 = MODC, MODC + KD, MODC + 2 * KD, MODC + 2 * KD + MH

C_ID, C_KEEP, C_BEFORE, C_COS, C_SIN, C_IOTA, C_TIE, C_END = 0, 128, 384, 512, 576, 640, 640 + TOK, 656 + TOK
SPILLS = TOK // SLOTS - 1


ROW_LOADS, SMALL_LOADS, LAYER_LOADS, STATE_OUTS = 5, 10, 3, 4
SPLIT = 6
R_LOG, R_E, R_SEL, R_T, R_IN2, R_W, R_GS, R_MASK, R_G, R_POS, R_X = range(11)


def shape_constants():
    t = np.arange(P)
    out = np.zeros((P, C_END), np.float32)
    out[:, C_ID:C_ID + P] = np.eye(P)
    out[:, C_KEEP:C_KEEP + P] = t[:, None] <= t[None, :]
    out[:, C_KEEP + P:C_KEEP + 2 * P] = t[:, None] >= t[None, :]
    out[:, C_BEFORE:C_BEFORE + P] = t[:, None] < t[None, :]
    half = HD // 2
    freqs = (np.float32(ROPE_BASE) ** (-np.arange(0, half, 2, dtype=np.float32) / np.float32(half)))
    row = (t // GRID_W).astype(np.float32)[:, None] * freqs[None, :]
    col = (t % GRID_W).astype(np.float32)[:, None] * freqs[None, :]
    out[:, C_COS:C_COS + HD] = np.concatenate([np.cos(row), np.cos(row), np.cos(col), np.cos(col)], 1)
    out[:, C_SIN:C_SIN + HD] = np.concatenate([-np.sin(row), np.sin(row), -np.sin(col), np.sin(col)], 1)
    out[:, C_IOTA:C_IOTA + TOK] = np.arange(TOK)[None, :]
    out[:, C_TIE:C_TIE + 16] = (np.arange(4)[None, :] < np.arange(4)[:, None]).reshape(1, 16)
    return out


def bank_plan():
    uses = [0] * 8
    fulls = [0] * 8
    plan = {}

    def put(key, bank, signalled=True):
        plan[key] = (bank, uses[bank], fulls[bank])
        uses[bank] += 1
        fulls[bank] += signalled

    put("cond", 7)
    for l in range(DEPTH):
        put(("rows", l), 6)
    for r in range(4):
        put(("x", r), r)
    put(("mod", 0), 7, signalled=False)
    for l in range(DEPTH):
        rot = [0]

        def turn(key):
            put((key, l), rot[0] % 4)
            rot[0] += 1

        put(("ssq1", l), 6)
        put(("gates", l), 4)
        for g in PROJ:
            for b in range(NB):
                turn((g, b))
        put(("gateT", l), 5)
        put(("scanT", l), 6)
        for d in range(2):
            put((("mrow", d, 0), l), 4)
            put((("mrow", d, 1), l), 5)
        for b in range(NB):
            turn(("mkT", b))
            turn(("mqT", b))
        for b in range(NB):
            turn(("ST", b))
        at = [0]

        def att(key):
            put((key, l), 4 + at[0] % 3)
            at[0] += 1

        for k in ("qT1", "kT1", "qT0", "kT0", "s10", "s11", "s12", "s13", "s00", "s01",
                  "p10", "p11", "p12", "p13", "p00", "p01", "o1", "o0"):
            att(k)
        for b in range(NB):
            for h in range(MH):
                if b == 1:
                    turn(("inter", h))
                turn(("num", b, h))
        for h in range(MH):
            turn(("C", h))
        turn("nT")
        for b in range(NB):
            turn(("mlT", b))
        if l + 1 < DEPTH:
            put(("mod", l + 1), 7, signalled=False)
        for i in range(4):
            turn(("mix", i))
        put(("ssq2", l), 6)
        for i in range(4):
            turn(("tok", i))
        put(("router", l), 6)
        put(("pos", l), 6)
        for i in range(4):
            put((("scat", i), l), 4 + i)
        plan["moe", l], plan["moe_full", l] = list(uses), list(fulls)
        for bank, n in enumerate((2 * PAIRS, 2 * PAIRS, PAIRS, PAIRS)):
            uses[bank] += n
            fulls[bank] += n
        for i in range(4):
            put((("y", i), l), 4 + i)
    for r in range(4):
        put(("out", r), r)
    return plan


PROJ = {"mk": (1280, 512), "mq": (768, 512), "mv": (1792, 512), "aq": (0, 512), "akv": (512, 256),
        "mo": (2304, 512)}


def weight_plan():
    n = 0
    last = [None] * RING
    plan = {}

    def put(key):
        nonlocal n
        plan[key] = (n % RING, n // RING, last[n % RING])
        last[n % RING] = key
        n += 1

    for i in range(MOD_SLOTS):
        put(("mod", 0, i))
    for l in range(DEPTH):
        for g in PROJ:
            put((g, l))
        if l + 1 < DEPTH:
            for i in range(MOD_SLOTS):
                put(("mod", l + 1, i))
        for i in range(2):
            put(("out", l, i))
        for i in range(RING):
            put(("expert", l, i))
        n += RING * (PAIRS - 1)
    return plan


def build(nc, t):
    banks, weights = bank_plan(), weight_plan()
    with ExitStack() as ctx:
        def sem(name):
            return ctx.enter_context(nc.semaphore(name))

        def sb(name, shape, dt=F32, where=ctx):
            return where.enter_context(nc.sbuf_tensor(name, shape, dt))

        ps = [ctx.enter_context(nc.psum_tensor(f"ps{i}", [P, 512], F32)) for i in range(8)]

        ring = sb("ring", [P, RING, KD * WB])
        cst = sb("cst", [P, C_END])
        ones = sb("ones", [P, P])
        eps = sb("eps", [P, 1])
        xT = sb("xT", [P, KD, TOK])
        hT = sb("hT", [P, KD, TOK])
        cT = sb("cT", [P, 2 * KD])
        cols = sb("cols", [P, DEPTH, ROWS_L])
        modc = sb("modc", [P, 2, MODC, NB])
        amp = sb("amp", [P, 2, 2, KD, NB])
        wg = sb("wg", [P, DEPTH, KD, NG])
        wr = sb("wr", [P, KD, E])
        gb = sb("gb", [P, DEPTH, NG])
        gqk = sb("gqk", [P, DEPTH, 2, HD])
        brt = sb("brt", [P, E])
        m0 = sb("m0", [64, DEPTH, NB])
        C0 = sb("C0", [P, 2 * MH, MD + 1])
        ck = sb("ck", [P, NKV * HD])
        cv = sb("cv", [P, NKV * HD])
        rstd = sb("rstd", [P, TOK])
        qc = sb("qc", [P, NB, 4, 8])
        qk_r = sb("qk_r", [P, NB, NQ + NKV])
        att = sb("att", [P, 4, 24])
        dn = sb("dn", [P, NB, MH, 2])
        hr = sb("hr", [P, NB, MH])
        ncol = sb("ncol", [P, 8])
        nst = sb("nst", [8, P])
        mnew = sb("mnew", [64, DEPTH])
        gpad = sb("gpad", [P, 2, NB, 64])
        zeros = sb("zeros", [P, P], BF16)
        count_i = sb("count_i", [P, DEPTH], I32)

        ident = cst[:, C_ID:C_ID + P]
        keep = cst[:, C_KEEP:C_KEEP + 2 * P].rearrange("p (d t) -> p d t", d=2)
        before = cst[:, C_BEFORE:C_BEFORE + P]

        with ExitStack() as mixer:
            work = sb("work", [P, NB * MH * 2 * (MD + 1)], where=mixer)
            qk = sb("qk", [P, NB, QW + NKV * HD], where=mixer)
            qkr = sb("qkr", [P, NB, QW], where=mixer)
            mk = sb("mk", [P, NB, ML], where=mixer)
            mq = sb("mq", [P, NB, ML], where=mixer)
            mv = sb("mv", [P, NB, MH, MD + 1], where=mixer)
            og = sb("og", [P, NB, ML], where=mixer)
            mkT = sb("mkT", [P, NB, MH, P], where=mixer)
            mqT = sb("mqT", [P, NB, MH, P], where=mixer)
            qT = sb("qT", [P, NB, 4, P], where=mixer)
            kT0 = sb("kT0", [P, NKV, P], where=mixer)
            kT1 = sb("kT1", [P, NKV, 2 * P], where=mixer)
            prob = sb("prob", [P, 12 * 256], where=mixer)
            pT1 = sb("pT1", [P, 4, 2, 2, P], where=mixer)
            W = sb("W", [P, 2, MH, NB, P], where=mixer)
        sq = work[:, 0:KD * TOK].rearrange("p (k t) -> p k t", k=KD)
        num = work[:, :].rearrange("p (b h d e) -> p b h d e", b=NB, h=MH, d=2)
        cat = hT
        kw = mq[:, :, :].rearrange("p d (h e) -> p d h e", h=MH)
        Cn = qk[:, :, :].rearrange("p b n -> p (b n)")[:, 0:8 * (MD + 1)].rearrange("p (g e) -> p g e", g=8)
        pT0 = mkT[:, :, :, :]
        rows = prob[0:64, 0:8 * P].rearrange("p (i b t) -> p i b t", i=4, b=NB)
        scans = prob[0:64, 8 * P:18 * P].rearrange("p (b q t) -> p b q t", b=NB, q=5)
        inter_s = pT1.ap().rearrange("p i j k t -> p (i j k t)")[:, 0:4 * (MD + 1)].rearrange("p (n d e) -> p n d e", n=2, d=2)

        with ExitStack() as experts:
            sq2 = sb("sq2", [P, KD, TOK], where=experts)
            htok = sb("htok", [P, NB, D], where=experts)
            pick = sb("pick", [P, NB, E, SLOTS], where=experts)
            gpick = sb("gpick", [P, NB, E, SLOTS], where=experts)
            scat = sb("scat", [P, PAIRS, TOK], where=experts)
            xe = sb("xe", [P, KD, P], where=experts)
            ex = sb("ex", [P, 2, KF, SLOTS], where=experts)
            hid = sb("hid", [P, 2, KF, SLOTS], where=experts)
            ye = sb("ye", [P, D], where=experts)
            rt = sb("rt", [P, 16, 32], where=experts)
            cmpa = sb("cmpa", [P, 8, 4, 4], where=experts)
            cmpb = sb("cmpb", [P, 8, 4, 4], where=experts)
            spick = sb("spick", [P, NB, SLOTS], where=experts)
            sgate = sb("sgate", [P, NB, SLOTS], where=experts)
            sscat = sb("sscat", [SLOTS, TOK], where=experts)
            sex = sb("sex", [P, KF, SLOTS], where=experts)
            shid = sb("shid", [P, KF, SLOTS], where=experts)
        xtok = ring[:, 5, 0:NB * D].rearrange("p (b d) -> p b d", b=NB)
        otok = sq2[:, :, :].rearrange("p k t -> p (k t)").rearrange("p (b d) -> p b d", b=NB)
        rowsin = prob[0:ROWS_L, 0:DEPTH * P].rearrange("p (l c) -> p l c", l=DEPTH)
        condr = prob[0:2 * KD, 1024:1024 + P]
        conde = prob[0:2 * KD, 1280:1280 + P]

        bank_full = [sem(f"bank_full{i}") for i in range(8)]
        bank_read = [sem(f"bank_read{i}") for i in range(8)]
        slot_landed = [sem(f"slot_landed{i}") for i in range(RING)]
        mod_read, gate_read, down_read = sem("mod_read"), sem("gate_read"), sem("down_read")
        dve_step, act_step = sem("dve_step"), sem("act_step")
        const_in, x_in, cond_in, rows_in, small_in = (sem(n) for n in (
            "const_in", "x_in", "cond_in", "rows_in", "small_in"))
        layer_in, state_out = sem("layer_in"), sem("state_out")
        names = ("ones_set cond_exp cond_silu mod_ready square_a square_v normed_g h_ready log1p scan_diff scan_exp "
                 "decay_exp decay_ready qk_sq qk_ssq qk_rstd qk_ready score_max prob_ready kw_ready head_ssq "
                 "head_rstd ml_ready n_ready c0_ready logit_max logit_exp mask_ready pick_ready gates_ready "
                 "gpick_ready silu_exp silu_step").split()
        (ones_set, cond_exp, cond_silu, mod_ready, square_a, square_v, normed_g, h_ready, log1p, scan_diff, scan_exp,
         decay_exp, decay_ready, qk_sq, qk_ssq, qk_rstd, qk_ready, score_max, prob_ready, kw_ready, head_ssq,
         head_rstd, ml_ready, n_ready, c0_ready, logit_max, logit_exp, mask_ready, pick_ready, gates_ready,
         gpick_ready, silu_exp, silu_step) = (sem(n) for n in names)
        (spill_turn, spill_landed, spill_pick, spill_gathered, spill_in, spill_hidden, spill_exp, spill_silu,
         spill_act, spill_down, spill_back) = (
            [sem(f"{n}{l}") for l in range(DEPTH)] for n in (
                "spill_turn", "spill_landed", "spill_pick", "spill_gathered", "spill_in", "spill_hidden", "spill_exp",
                "spill_silu", "spill_act", "spill_down", "spill_back"))
        y_out, kv_out, m0_clear, eps_set = sem("y_out"), sem("kv_out"), sem("m0_clear"), sem("eps_set")

        def full(eng, key):
            bank, _, n = banks[key]
            eng.wait_ge(bank_full[bank], n + 1)
            return ps[bank]

        def taken(eng, *keys):
            for key in keys:
                bank, n, _ = banks[key]
                eng.wait_ge(bank_read[bank], n + 1)

        def free(key):
            return bank_read[banks[key][0]]

        def stepper(eng, done_steps):
            noted = [0]

            def note(ins):
                noted[0] += 1
                ins.then_inc(done_steps, 1)

            def settle():
                eng.wait_ge(done_steps, noted[0])

            def step(ins):
                note(ins)
                settle()

            return note, settle, step

        def overflow(eng, l):
            taken(eng, ("pos", l))
            return eng.value_load(count_i[0:1, l:l + 1], min_val=0, max_val=TOK) > SLOTS

        SPILL_BLOCKS = (0, 1, 4)

        def spill_weights(l, k):
            return ring[:, weights["expert", l, SPILL_BLOCKS[k]][0], :]

        def per_col(ap, width):
            return ap.unsqueeze(len(ap.shape)).broadcast_to([*ap.shape, width])

        def repeat(ap, n):
            return ap.unsqueeze(1).broadcast_to([ap.shape[0], n, *ap.shape[1:]])

        block = ctx.enter_context(nc.Block())

        @block.sync
        def _(sp):
            w_mod = t["w_mod"].rearrange("l (k p) n -> l p k n", p=P)
            w_in = t["w_in"].rearrange("l (k p) n -> l p k n", p=P)
            w_out = t["w_out"].rearrange("l (k p) n -> l p k n", p=P)
            w_gate = t["w_e_gate"].rearrange("l e (k p) n -> l e p k n", p=P)
            w_up = t["w_e_up"].rearrange("l e (k p) n -> l e p k n", p=P)
            w_down = t["w_e_down"].rearrange("l e (k p) n -> l e p k n", p=P)

            def expert_read(l, i, p):
                base = banks["moe_full", l]
                if i in (0, 2):
                    sp.wait_ge(gate_read, 2 * p + (E * l + i // 2 + 1))
                elif i in (1, 3):
                    sp.wait_ge(bank_full[1], 2 * p + (base[1] + i // 2 + 1))
                elif i == 4:
                    sp.wait_ge(down_read, p + (PAIRS * l + 1))
                else:
                    sp.wait_ge(bank_full[3], p + (base[3] + 1))

            def was_read(key):
                if key[0] == "mod":
                    sp.wait_ge(mod_read, MOD_SLOTS * key[1] + key[2] + 1)
                elif key[0] == "out":
                    full(sp, (("mix", 2 * key[2] + 1), key[1]))
                elif key[0] == "expert":
                    expert_read(key[1], key[2], PAIRS - 1)
                else:
                    full(sp, ((key[0], 1), key[1]))

            def load(key, src, width=WB):
                slot, _, last = weights[key]
                if last is not None:
                    was_read(last)
                elif slot == RING - 1:
                    taken(sp, ("x", 0), ("x", 1), ("x", 2), ("x", 3))
                dst = ring[:, slot, 0:KD * width].rearrange("p (k n) -> p k n", k=KD)
                sp.dma_start(dst, src).then_inc(slot_landed[slot], 16)

            for i in range(MOD_SLOTS):
                load(("mod", 0, i), w_mod[0, :, :, i * WB:(i + 1) * WB])
            for l in range(DEPTH):
                for g, (c0, width) in PROJ.items():
                    load((g, l), w_in[l, :, :, c0:c0 + width], width)
                if l + 1 < DEPTH:
                    for i in range(MOD_SLOTS):
                        load(("mod", l + 1, i), w_mod[l + 1, :, :, i * WB:(i + 1) * WB])
                for i in range(2):
                    load(("out", l, i), w_out[l, :, :, i * WB:(i + 1) * WB])
                blocks = ((w_gate, 0, KD), (w_up, 0, KD), (w_gate, 1, KD), (w_up, 1, KD), (w_down, 0, KF), (w_down, 1, KF))

                def pair_loads(p):
                    for i, (w, j, k) in enumerate(blocks):
                        slot, _, last = weights["expert", l, i]
                        if isinstance(p, int):
                            was_read(last)
                        else:
                            expert_read(l, i, p - 1)
                        sp.dma_start(ring[:, slot, :].rearrange("p (k n) -> p k n", k=k),
                                     w[l, 2 * p + j]).then_inc(slot_landed[slot], 16)

                pair_loads(0)
                with sp.Fori(1, PAIRS) as p:
                    pair_loads(p)
                with sp.If(overflow(sp, l)):
                    for i in SPILL_BLOCKS:
                        expert_read(l, i, PAIRS - 1)
                    with sp.Fori(0, E) as e:
                        sp.wait_ge(spill_turn[l], SPILLS * e + 1)
                        for k, w in enumerate((w_gate, w_up, w_down)):
                            sp.dma_start(spill_weights(l, k).rearrange("p (k n) -> p k n", k=(KD, KD, KF)[k]),
                                         w[l, e]).then_inc(spill_landed[l], 16)
                    sp.wait_ge(spill_turn[l], SPILLS * E + 1)
            for b, name in enumerate(("y_prompt", "y_sample")):
                for half in range(2):
                    taken(sp, ("out", 2 * b + half))
                sp.dma_start(t[name][0], otok[:, b, :]).then_inc(y_out, 16)
            sp.wait_ge(y_out, 16 * NB)

        @block.tensor
        def _(pe):
            def begin(key):
                bank, n, _ = banks[key]
                if n > 0:
                    pe.wait_ge(bank_read[bank], n)
                return ps[bank]

            def done(key, ins):
                ins.then_inc(bank_full[banks[key][0]], 1)

            def landed(key, p=0):
                slot, n, _ = weights[key]
                pe.wait_ge(slot_landed[slot], p * 16 + 16 * (n + 1))
                return ring[:, slot, :]

            def modulation(l, i):
                if i == 0:
                    begin(("mod", l))
                w = landed(("mod", l, i)).rearrange("p (k n) -> p k n", k=KD)
                for j in range(4):
                    c = 2 * (4 * i + j)
                    for k in range(KD):
                        mm = pe.matmul(ps[7][:, c:c + 2], w[:, k, j * P:(j + 1) * P], cT[:, k:2 * KD:KD],
                                       start=(k == 0), stop=(k == KD - 1))
                mm.then_inc(mod_read, 1)

            def norm_sums(key, square, n):
                bank = begin(key)
                pe.wait_ge(square_a, n)
                pe.wait_ge(square_v, n)
                for k in range(KD):
                    mm = pe.matmul(bank[:, 0:TOK], ones[:, :], square[:, k, :], start=(k == 0), stop=(k == KD - 1))
                done(key, mm)

            pe.wait_ge(const_in, 16)
            pe.wait_ge(ones_set, 1)
            bank = begin("cond")
            pe.wait_ge(cond_silu, 1)
            done("cond", pe.transpose(bank[:, 0:2 * KD], condr, ident[0:2 * KD, 0:2 * KD]))
            pe.wait_ge(rows_in, 16 * ROW_LOADS * DEPTH)
            for l in range(DEPTH):
                bank = begin(("rows", l))
                done(("rows", l), pe.transpose(bank[:, 0:ROWS_L], rowsin[:, l, :], ident[0:ROWS_L, 0:ROWS_L]))
            pe.wait_ge(x_in, 16 * NB)
            for r in range(4):
                b, half = r // 2, r % 2
                bank = begin(("x", r))
                for k in range(4):
                    c = (4 * half + k) * P
                    mm = pe.transpose(bank[:, k * P:(k + 1) * P], xtok[:, b, c:c + P], ident)
                done(("x", r), mm)
            taken(pe, "cond")
            for i in range(MOD_SLOTS):
                modulation(0, i)

            for l in range(DEPTH):
                turns = iter(range(MOD_SLOTS if l + 1 < DEPTH else 0))

                def next_modulation(count):
                    for _, i in zip(range(count), turns):
                        modulation(l + 1, i)

                norm_sums(("ssq1", l), sq, 2 * l + 1)

                pe.wait_ge(h_ready, 2 * (2 * l + 1))
                pe.wait_ge(small_in, 16 * SMALL_LOADS)
                bank = begin(("gates", l))
                for b in range(NB):
                    for k in range(KD):
                        mm = pe.matmul(bank[:, b * NG:(b + 1) * NG], hT[:, k, b * P:(b + 1) * P], wg[:, l, k, :],
                                       start=(k == 0), stop=(k == KD - 1))
                done(("gates", l), mm)

                def project(g):
                    _, width = PROJ[g]
                    w = landed((g, l))[:, 0:KD * width].rearrange("p (k n) -> p k n", k=KD)
                    for b in range(NB):
                        bank = begin(((g, b), l))
                        for k in range(KD):
                            mm = pe.matmul(bank[:, 0:width], hT[:, k, b * P:(b + 1) * P], w[:, k, :],
                                           start=(k == 0), stop=(k == KD - 1))
                        done(((g, b), l), mm)

                def gate_rows():
                    bank = begin(("gateT", l))
                    taken(pe, ("gates", l))
                    for i in range(2):
                        for b in range(NB):
                            c = (2 * i + b) * P
                            mm = pe.transpose(bank[0:64, c:c + P], gpad[:, i, b, :], ident)
                    done(("gateT", l), mm)

                def scan_columns():
                    bank = begin(("scanT", l))
                    pe.wait_ge(scan_exp, l + 1)
                    for b in range(NB):
                        for q in range(4):
                            c = (4 * b + q) * 64
                            mm = pe.transpose(bank[:, c:c + 64], scans[:, b, 1 + q, :], ident[0:64, 0:64])
                    done(("scanT", l), mm)

                def max_rows(d):
                    for i in range(2):
                        bank = begin((("mrow", d, i), l))
                        for j in range(2):
                            r = 32 * d + 2 * i + j
                            mm = pe.matmul(bank[:, j * TOK:(j + 1) * TOK], ident[0:64, r:r + 1].broadcast_to([64, P]),
                                           scans[:, :, 0, :], start=True, stop=True)
                        done((("mrow", d, i), l), mm)

                project("mk")
                gate_rows()
                project("mq")
                project("mv")
                project("aq")
                scan_columns()
                max_rows(0)
                project("akv")
                max_rows(1)
                project("mo")

                for b in range(NB):
                    for key, src, ready in (("mkT", mk, "mk"), ("mqT", mq, "mq")):
                        bank = begin(((key, b), l))
                        taken(pe, ((ready, b), l))
                        for h in range(MH):
                            mm = pe.transpose(bank[:, h * P:(h + 1) * P], src[:, b, h * MD:(h + 1) * MD], ident)
                        done(((key, b), l), mm)
                next_modulation(1)
                for b in range(NB):
                    bank = begin((("ST", b), l))
                    taken(pe, (("mkT", b), l), (("mqT", b), l))
                    for h in range(MH):
                        mm = pe.matmul(bank[:, h * P:(h + 1) * P], mkT[:, b, h, :], mqT[:, b, h, :],
                                       start=True, stop=True)
                    done((("ST", b), l), mm)
                next_modulation(2)

                pe.wait_ge(layer_in, 16 * LAYER_LOADS * (l + 1))
                for b in (1, 0):
                    bank = begin((f"qT{b}", l))
                    pe.wait_ge(qk_ready, NB * l + b + 1)
                    for j in range(4):
                        mm = pe.transpose(bank[:, j * P:(j + 1) * P], qkr[:, b, j * P:(j + 1) * P], ident)
                    done((f"qT{b}", l), mm)
                    bank = begin((f"kT{b}", l))
                    for g in range(NKV):
                        c = NQ * HD + g * HD
                        own = qkr[:, b, c:c + HD]
                        blocks = (own,) if b == 0 else (ck[:, g * HD:(g + 1) * HD], own)
                        for i, src in enumerate(blocks):
                            at = (g * len(blocks) + i) * P
                            for half in range(2):
                                mm = pe.matmul(bank[64 * half:64 * half + 64, at:at + P], src, ident,
                                               start=True, stop=True)
                    done((f"kT{b}", l), mm)
                next_modulation(1)
                taken(pe, ("qT1", l), ("kT1", l))
                for i in range(4):
                    bank = begin((f"s1{i}", l))
                    par, g = i % 2, i // 2
                    for j in range(2):
                        mm = pe.matmul(bank[:, j * TOK:(j + 1) * TOK], qT[64 * par:64 * par + 64, 1, 2 * g + j, :],
                                       kT1[64 * par:64 * par + 64, g, :], start=True, stop=True)
                    done((f"s1{i}", l), mm)
                    next_modulation(i % 2)
                taken(pe, ("qT0", l), ("kT0", l))
                for par in range(2):
                    bank = begin((f"s0{par}", l))
                    for j in range(4):
                        mm = pe.matmul(bank[:, j * P:(j + 1) * P], qT[64 * par:64 * par + 64, 0, j, :],
                                       kT0[64 * par:64 * par + 64, j // 2, :], start=True, stop=True)
                    done((f"s0{par}", l), mm)
                next_modulation(1)
                for i in range(4):
                    bank = begin((f"p1{i}", l))
                    pe.wait_ge(prob_ready, 6 * l + i + 1)
                    for n in range(4):
                        c = i * 512 + n * P
                        mm = pe.transpose(bank[:, n * P:(n + 1) * P], prob[:, c:c + P], ident)
                    done((f"p1{i}", l), mm)
                for par in range(2):
                    bank = begin((f"p0{par}", l))
                    pe.wait_ge(prob_ready, 6 * l + 5 + par)
                    for j in range(4):
                        c = (4 + par) * 512 + j * P
                        mm = pe.transpose(bank[:, j * P:(j + 1) * P], prob[:, c:c + P], ident)
                    done((f"p0{par}", l), mm)
                taken(pe, (("akv", 0), l), (("akv", 1), l))
                bank = begin(("o1", l))
                for i in range(4):
                    taken(pe, (f"p1{i}", l))
                    par, g = i % 2, i // 2
                    for j in range(2):
                        for kb in range(2):
                            v = cv[:, g * HD:(g + 1) * HD] if kb == 0 else qk[:, 1, QW + g * HD:QW + (g + 1) * HD]
                            mm = pe.matmul(bank[64 * par:64 * par + 64, (2 * g + j) * P:(2 * g + j + 1) * P],
                                           v, pT1[:, i, j, kb, :], start=(kb == 0), stop=(kb == 1))
                done(("o1", l), mm)
                bank = begin(("o0", l))
                for par in range(2):
                    taken(pe, (f"p0{par}", l))
                    for j in range(4):
                        g = j // 2
                        mm = pe.matmul(bank[64 * par:64 * par + 64, j * P:(j + 1) * P],
                                       qk[:, 0, QW + g * HD:QW + (g + 1) * HD], pT0[:, par, j, :],
                                       start=True, stop=True)
                done(("o0", l), mm)

                taken(pe, (("mv", 0), l), (("mv", 1), l))
                for b in range(NB):
                    taken(pe, (("ST", b), l))
                    if b == 1:
                        pe.wait_ge(c0_ready, l + 1)
                    for h in range(MH):
                        if b == 1:
                            bank = begin((("inter", h), l))
                            for d in range(2):
                                mm = pe.matmul(bank[:, d * (MD + 1):(d + 1) * (MD + 1)], mqT[:, 1, h, :],
                                               C0[:, d * MH + h, :], start=True, stop=True)
                            done((("inter", h), l), mm)
                        bank = begin((("num", b, h), l))
                        for d in range(2):
                            mm = pe.matmul(bank[:, d * (MD + 1):(d + 1) * (MD + 1)], W[:, d, h, b, :], mv[:, b, h, :],
                                           start=True, stop=True)
                        done((("num", b, h), l), mm)
                pe.wait_ge(kw_ready, 2 * (l + 1))
                for h in range(MH):
                    bank = begin((("C", h), l))
                    for d in range(2):
                        mm = pe.matmul(bank[:, d * (MD + 1):(d + 1) * (MD + 1)], kw[:, d, h, :], mv[:, 0, h, :],
                                       start=True, stop=True)
                    done((("C", h), l), mm)
                next_modulation(2)
                bank = begin(("nT", l))
                pe.wait_ge(n_ready, l + 1)
                done(("nT", l), pe.transpose(bank[0:8, 0:P], ncol[:, :], ident))
                for b in range(NB):
                    bank = begin((("mlT", b), l))
                    pe.wait_ge(ml_ready, NB * l + b + 1)
                    for h in range(MH):
                        mm = pe.transpose(bank[:, h * P:(h + 1) * P], og[:, b, h * MD:(h + 1) * MD], ident)
                    done((("mlT", b), l), mm)
                    next_modulation(1 if b == 0 else MOD_SLOTS)

                taken(pe, ("o1", l), ("o0", l), (("mlT", 0), l), (("mlT", 1), l))
                for s in range(2):
                    w = landed(("out", l, s)).rearrange("p (k n) -> p k n", k=KD)
                    for i in (2 * s, 2 * s + 1):
                        bank = begin((("mix", i), l))
                        for j in range(2):
                            c = (2 * (i % 2) + j) * P
                            for k in range(KD):
                                mm = pe.matmul(bank[:, j * TOK:(j + 1) * TOK], w[:, k, c:c + P], cat[:, k, :],
                                               start=(k == 0), stop=(k == KD - 1))
                        done((("mix", i), l), mm)

                norm_sums(("ssq2", l), sq2, 2 * l + 2)
                pe.wait_ge(h_ready, 2 * (2 * l + 2))
                bank = begin(("router", l))
                for b in range(NB):
                    for k in range(KD):
                        mm = pe.matmul(bank[:, b * E:(b + 1) * E], hT[:, k, b * P:(b + 1) * P], wr[:, k, :],
                                       start=(k == 0), stop=(k == KD - 1))
                done(("router", l), mm)
                for i in range(4):
                    b, half = i // 2, i % 2
                    bank = begin((("tok", i), l))
                    for k in range(4):
                        mm = pe.transpose(bank[:, k * P:(k + 1) * P], hT[:, 4 * half + k, b * P:(b + 1) * P], ident)
                    done((("tok", i), l), mm)
                bank = begin(("pos", l))
                pe.wait_ge(mask_ready, l + 1)
                m = [rt[:, R_MASK, b * E:(b + 1) * E] for b in range(NB)]
                pe.matmul(bank[:, 0:E], before, m[0], start=True, stop=True)
                pe.matmul(bank[:, E:2 * E], before, m[1], start=True, stop=False)
                pe.matmul(bank[:, E:2 * E], ones[:, :], m[0], start=False, stop=True)
                pe.matmul(bank[:, 2 * E:3 * E], ones[:, :], m[0], start=True, stop=False)
                mm = pe.matmul(bank[:, 2 * E:3 * E], ones[:, :], m[1], start=False, stop=True)
                done(("pos", l), mm)

                base = banks["moe", l]

                def gather(p, half):
                    pe.wait_ge(bank_read[0], 2 * p + (base[0] + half))
                    for k in range(4):
                        for b in range(NB):
                            c = (4 * half + k) * P
                            mm = pe.matmul(ps[0][:, k * P:(k + 1) * P], htok[:, b, c:c + P],
                                           pick[:, b, bass.ds(2 * p, 2), :].rearrange("p e c -> p (e c)"),
                                           start=(b == 0), stop=(b == NB - 1))
                    mm.then_inc(bank_full[0], 1)

                def gate_up(p, j):
                    if j == 0:
                        pe.wait_ge(bank_read[0], 2 * p + (base[0] + 2))
                    pe.wait_ge(bank_read[1], 2 * p + (base[1] + j))
                    for u in range(2):
                        w = landed(("expert", l, 2 * j + u), p).rearrange("p (k n) -> p k n", k=KD)
                        for f in range(KF):
                            c = (u * KF + f) * SLOTS
                            for k in range(KD):
                                mm = pe.matmul(ps[1][:, c:c + SLOTS], w[:, k, f * P:(f + 1) * P],
                                               xe[:, k, j * SLOTS:(j + 1) * SLOTS],
                                               start=(k == 0), stop=(k == KD - 1))
                        mm.then_inc((gate_read, bank_full[1])[u], 1)

                def down(p, j):
                    w = landed(("expert", l, 4 + j), p).rearrange("p (k n) -> p k n", k=KF)
                    pe.wait_ge(bank_read[1], 2 * p + (base[1] + j + 1))
                    if j == 0:
                        pe.wait_ge(bank_read[2], p + base[2])
                        pe.wait_ge(bank_read[3], p + base[3])
                    for half in range(2):
                        for k in range(KF):
                            mm = pe.matmul(ps[2 + half][64 * j:64 * j + 64, :], hid[:, j, k, :],
                                           w[:, k, half * 512:(half + 1) * 512], start=(k == 0), stop=(k == KF - 1))
                        if j == 1:
                            mm.then_inc(bank_full[2 + half], 1)
                        elif half == 1:
                            mm.then_inc(down_read, 1)

                def scatter(p):
                    pe.wait_ge(bank_read[2], p + (base[2] + 1))
                    pe.wait_ge(bank_read[3], p + (base[3] + 1))
                    for dj in range(KD):
                        mm = pe.matmul(ps[4 + dj // 2][:, (dj % 2) * TOK:(dj % 2 + 1) * TOK], ye[:, dj * P:(dj + 1) * P],
                                       scat[:, bass.ds(p, 1), :].rearrange("p a t -> p (a t)"),
                                       start=False, stop=False, skip_group_check=True)
                    return mm

                def pair(p, first=False, last=False):
                    gate_up(p, 0)
                    if not first:
                        scatter(p - 1)
                    gate_up(p, 1)
                    if not last:
                        gather(p + 1, 0)
                    down(p, 0)
                    if not last:
                        gather(p + 1, 1)
                    down(p, 1)

                pe.wait_ge(pick_ready, l + 1)
                taken(pe, *[(("tok", i), l) for i in range(4)])
                gather(0, 0)
                gather(0, 1)
                pe.wait_ge(gpick_ready, l + 1)
                for i in range(4):
                    bank = begin((("scat", i), l))
                    for j in range(2):
                        for b in range(NB):
                            e = 2 * (2 * i + j)
                            mm = pe.transpose(bank[:, j * TOK + b * P:j * TOK + (b + 1) * P],
                                              gpick[:, b, e:e + 2, :].rearrange("p e c -> p (e c)"), ident)
                    done((("scat", i), l), mm)
                taken(pe, *[(("scat", i), l) for i in range(4)])
                for i in range(4):
                    begin((("y", i), l))
                    pe.matmul(ps[4 + i][:, :], zeros[:, :], zeros[:, 0:1].broadcast_to([P, 512]), start=True, stop=False, skip_group_check=True)
                pair(0, first=True)
                with pe.Fori(1, PAIRS - 1) as p:
                    pair(p)
                pair(PAIRS - 1, last=True)
                scatter(PAIRS - 1)

                def spill(e, c):
                    n = SPILLS * e + c + 1
                    pe.wait_ge(spill_pick[l], n)
                    for k in range(KD):
                        for b in range(NB):
                            pe.matmul(ps[0][:, k * SLOTS:(k + 1) * SLOTS], htok[:, b, k * P:(k + 1) * P], spick[:, b, :],
                                      start=(b == 0), stop=(b == NB - 1))
                    for b in range(NB):
                        mm = pe.transpose(ps[1][0:SLOTS, b * P:(b + 1) * P], sgate[:, b, :], ident)
                    mm.then_inc(spill_gathered[l], 1)
                    pe.wait_ge(spill_in[l], n)
                    pe.wait_ge(spill_landed[l], 48 * e + 48)
                    for u in range(2):
                        w = spill_weights(l, u).rearrange("p (k n) -> p k n", k=KD)
                        for f in range(KF):
                            for k in range(KD):
                                mm = pe.matmul(ps[2][:, (u * KF + f) * SLOTS:(u * KF + f + 1) * SLOTS],
                                               w[:, k, f * P:(f + 1) * P],
                                               xe[:, k // 2, (k % 2) * SLOTS:(k % 2 + 1) * SLOTS],
                                               start=(k == 0), stop=(k == KD - 1))
                    mm.then_inc(spill_hidden[l], 1)
                    pe.wait_ge(spill_act[l], n)
                    w = spill_weights(l, 2).rearrange("p (k n) -> p k n", k=KF)
                    for half in range(2):
                        for k in range(KF):
                            mm = pe.matmul(ps[half][0:SLOTS, :], shid[:, k, :], w[:, k, half * 512:(half + 1) * 512],
                                           start=(k == 0), stop=(k == KF - 1))
                    mm.then_inc(spill_down[l], 1)
                    pe.wait_ge(spill_back[l], n)
                    for dj in range(KD):
                        mm = pe.matmul(ps[4 + dj // 2][:, (dj % 2) * TOK:(dj % 2 + 1) * TOK],
                                       ye[0:SLOTS, dj * P:(dj + 1) * P], sscat[:, :],
                                       start=False, stop=False, skip_group_check=True)
                    mm.then_inc(spill_turn[l], 1)

                with pe.If(overflow(pe, l)):
                    with pe.Fori(0, E) as e:
                        with pe.Fori(0, SPILLS) as c:
                            spill(e, c)
                for i in range(4):
                    done((("y", i), l), pe.matmul(ps[4 + i][:, :], zeros[:, :], zeros[:, 0:1].broadcast_to([P, 512]), start=False, stop=True,
                                                  skip_group_check=True))

            taken(pe, (("y", 3), DEPTH - 1))
            for r in range(4):
                b, half = r // 2, r % 2
                bank = begin(("out", r))
                for k in range(4):
                    mm = pe.transpose(bank[:, k * P:(k + 1) * P], xT[:, 4 * half + k, b * P:(b + 1) * P], ident)
                done(("out", r), mm)

        @block.scalar
        def _(act):
            note, settle, step = stepper(act, act_step)
            act.dma_start(condr[0:KD, :], t["c_ctx"].rearrange("(k c) -> k c", k=KD)).then_inc(cond_in, 16)
            act.dma_start(condr[KD:2 * KD, :], t["c"].rearrange("a (k c) -> (a k) c", k=KD)).then_inc(cond_in, 16)
            act.dma_start(cst[:, :], t["constants"]).then_inc(const_in, 16)
            for l in range(DEPTH):
                act.dma_start(rowsin[0:MODC, l, :], t["b_mod"][l].rearrange("(k c) -> k c", c=P)).then_inc(rows_in, 16)
                act.dma_start(rowsin[A_GMIX:A_GFFN, l, :], t["g_mix"][l].rearrange("(k c) -> k c", c=P)).then_inc(rows_in, 16)
                act.dma_start(rowsin[A_GFFN:A_GMH, l, :], t["g_ffn"][l].rearrange("(k c) -> k c", c=P)).then_inc(rows_in, 16)
                act.dma_start(rowsin[A_GMH:A_N0, l, :], t["g_mh"][l].rearrange("(k c) -> k c", c=P)).then_inc(rows_in, 16)
                act.dma_start(rowsin[A_N0:ROWS_L, l, :], t["state_n"][0, l].rearrange("a h c -> (a h) c")).then_inc(rows_in, 16)
            for b, name in enumerate(("x_prompt", "x_sample")):
                act.dma_start(xtok[:, b, :], t[name][0]).then_inc(x_in, 16)
            for l in range(DEPTH):
                act.dma_start(wg[:, l, :, :], t["w_in"][l].rearrange("(k p) n -> p k n", p=P)[:, :, GATE0:GATE0 + NG])\
                   .then_inc(small_in, 16)
            act.dma_start(wr[:, :, :], t["w_router"].rearrange("(k p) n -> p k n", p=P)).then_inc(small_in, 16)
            act.dma_start(gb[:, :, 0:8], t["b_igate"].rearrange("l a h -> l (a h)").partition_broadcast(P)).then_inc(small_in, 16)
            act.dma_start(gb[:, :, 8:16], t["b_fgate"].rearrange("l a h -> l (a h)").partition_broadcast(P)).then_inc(small_in, 16)
            act.dma_start(gqk[:, :, 0, :], t["g_q"].partition_broadcast(P)).then_inc(small_in, 16)
            act.dma_start(gqk[:, :, 1, :], t["g_k"].partition_broadcast(P)).then_inc(small_in, 16)
            act.dma_start(brt[:, :], t["b_router"].partition_broadcast(P)).then_inc(small_in, 16)
            act.wait_ge(m0_clear, 1)
            for d in range(2):
                act.dma_start(m0[32 * d:32 * d + MH, :, 1], t["state_m"][0, :, d, :].rearrange("l h -> h l"),
                              allow_slow_non_contiguous=True).then_inc(small_in, 16)

            act.wait_ge(cond_in, 32)
            act.activation(conde, condr, ACT.Exp, scale=-1.0).then_inc(cond_exp, 1)
            for r in range(4):
                b, half = r // 2, r % 2
                bank = full(act, ("x", r))
                act.activation(xT[:, 4 * half:4 * half + 4, b * P:(b + 1) * P], bank[:, :].rearrange("p (k t) -> p k t", k=4),
                               ACT.Copy).then_inc(free(("x", r)), 1)
            act.wait_ge(eps_set, 1)

            def power(dst, src, width):
                step(act.activation(dst, src, ACT.Ln, scale=1.0 / width, bias=eps[0:dst.shape[0], :]))
                return act.activation(dst, dst, ACT.Exp, scale=-0.5)

            def normalise(l, which, ready, square):
                taken(act, *ready)
                act.activation(square[:, 0:4, :], xT[:, 0:4, :], ACT.Square).then_inc(square_a, 1)
                key = (f"ssq{which + 1}", l)
                bank = full(act, key)
                step(act.activation(rstd[:, :], bank[:, 0:TOK], ACT.Ln, scale=1.0 / D, bias=eps[:, :]))
                act.activation(rstd[:, :], rstd[:, :], ACT.Exp, scale=-0.5).then_inc(free(key), 1)
                act.wait_ge(normed_g, 2 * l + which + 1)
                act.wait_ge(mod_ready, l + 1)
                for k in range(SPLIT, KD):
                    for b in range(NB):
                        ins = act.activation(hT[:, k, b * P:(b + 1) * P], square[:, k, b * P:(b + 1) * P], ACT.Identity,
                                             scale=amp[:, l % 2, which, k, b:b + 1],
                                             bias=modc[:, l % 2, 3 * KD * which + k, b:b + 1])
                ins.then_inc(h_ready, 1)

            for l in range(DEPTH):
                if l > 0:
                    act.wait_ge(state_out, 16 * STATE_OUTS * l)
                normalise(l, 0, [("x", r) for r in range(4)] if l == 0 else [(("y", 3), l - 1)], sq)

                for b in range(NB):
                    key = (("mk", b), l)
                    bank = full(act, key)
                    act.activation(mk[:, b, :], bank[:, :], ACT.Copy, scale=float(MD) ** -0.5).then_inc(free(key), 1)
                key = ("gateT", l)
                bank = full(act, key)
                act.activation(rows[:, 0:2, :, :].rearrange("p i b t -> p (i b t)"), bank[0:64, :], ACT.Copy).then_inc(free(key), 1)
                taken(act, key)
                step(act.activation(rows[:, 2, :, :], rows[:, 1, :, :], ACT.Abs))
                step(act.activation(rows[:, 2, :, :], rows[:, 2, :, :], ACT.Exp, scale=-1.0))
                act.activation(rows[:, 2, :, :], rows[:, 2, :, :], ACT.Ln, bias=1.0).then_inc(log1p, 1)
                act.wait_ge(scan_diff, l + 1)
                for b in range(NB):
                    ins = act.activation(scans[:, b, 2:5, :], scans[:, b, 2:5, :], ACT.Exp)
                ins.then_inc(scan_exp, 1)
                for b in range(NB):
                    key = (("mv", b), l)
                    bank = full(act, key)
                    act.activation(mv[:, b, :, 0:MD], bank[:, :].rearrange("p (h e) -> p h e", h=MH), ACT.Copy).then_inc(free(key), 1)
                for b in range(NB):
                    key = (("aq", b), l)
                    bank = full(act, key)
                    act.activation(qk[:, b, 0:NQ * HD], bank[:, :], ACT.Copy).then_inc(free(key), 1)

                def decay(d):
                    taken(act, (("mrow", d, 0), l), (("mrow", d, 1), l))
                    act.activation(W[:, d, :, :, :], W[:, d, :, :, :], ACT.Exp, scale=-1.0).then_inc(decay_exp, 1)

                decay(0)
                decay(1)
                act.wait_ge(qk_ssq, l + 1)
                power(qk_r[:, :, :], qk_r[:, :, :], HD).then_inc(qk_rstd, 1)
                for b in range(NB):
                    key = (("mo", b), l)
                    bank = full(act, key)
                    act.activation(og[:, b, :], bank[:, :], ACT.Exp, scale=-1.0).then_inc(free(key), 1)
                for b in range(NB):
                    key = (("mkT", b), l)
                    bank = full(act, key)
                    act.activation(mkT[:, b, :, :].rearrange("p h t -> p (h t)"), bank[:, :], ACT.Copy).then_inc(free(key), 1)
                for b in (1, 0):
                    key = (f"qT{b}", l)
                    bank = full(act, key)
                    act.activation(qT[:, b, :, :].rearrange("p h t -> p (h t)"), bank[:, :], ACT.Copy).then_inc(free(key), 1)

                def exponent(i):
                    par = i - 4
                    key = (f"s1{i}", l) if i < 4 else (f"s0{par}", l)
                    heads, width = (2, TOK) if i < 4 else (4, P)
                    act.wait_ge(score_max, 6 * l + i + 1)
                    bank = full(act, key)
                    for j in range(heads):
                        c = i * 512 + j * width
                        note(act.activation(prob[:, c:c + width], bank[:, j * width:(j + 1) * width], ACT.Exp,
                                                 bias=att[:, 1, 4 * i + j:4 * i + j + 1], scale=HD ** -0.5,
                                                 accum_out=att[:, 2, 4 * i + j:4 * i + j + 1]))
                    settle()
                    act.activation(att[:, 3, 4 * i:4 * i + heads], att[:, 2, 4 * i:4 * i + heads], ACT.Copy).then_inc(free(key), 1)

                def spread(key, dst):
                    bank = full(act, key)
                    act.activation(dst, bank[:, :], ACT.Copy).then_inc(free(key), 1)

                for i in range(6):
                    exponent(i)
                spread(("p10", l), pT1[:, 0, :, :, :].rearrange("p j k t -> p (j k t)"))
                spread(("p12", l), pT1[:, 2, :, :, :].rearrange("p j k t -> p (j k t)"))
                spread(("p00", l), pT0[:, 0, :, :].rearrange("p j t -> p (j t)"))
                key = ("o1", l)
                bank = full(act, key)
                act.activation(cat[:, 0:4, P:2 * P], bank[:, :].rearrange("p (k t) -> p k t", k=4), ACT.Copy).then_inc(free(key), 1)

                for h in range(MH):
                    key = (("inter", h), l)
                    bank = full(act, key)
                    if h >= 2:
                        taken(act, (("num", 1, h - 2), l))
                    for d in range(2):
                        ins = act.activation(inter_s[:, h % 2, d, :], bank[:, d * (MD + 1):(d + 1) * (MD + 1)], ACT.Copy,
                                             scale=qc[:, 1, 1, d * MH + h:d * MH + h + 1])
                    ins.then_inc(free(key), 1)
                act.wait_ge(kv_out, 32 * (l + 1))
                for h in range(MH):
                    key = (("C", h), l)
                    bank = full(act, key)
                    act.activation(Cn.rearrange("p (d h) e -> p d h e", d=2)[:, :, h, :],
                                   bank[:, 0:2 * (MD + 1)].rearrange("p (d e) -> p d e", d=2), ACT.Copy).then_inc(free(key), 1)
                act.wait_ge(head_ssq, NB * l + 1)
                power(hr[:, 0, :], hr[:, 0, :], MD).then_inc(head_rstd, 1)
                act.wait_ge(head_ssq, NB * l + 2)
                power(hr[:, 1, :], hr[:, 1, :], MD).then_inc(head_rstd, 1)
                key = (("mlT", 0), l)
                bank = full(act, key)
                for h in range(MH):
                    ins = act.activation(cat[:, MH + h, 0:P], bank[:, h * P:(h + 1) * P], ACT.Copy,
                                         scale=cols[:, l, A_GMH + h:A_GMH + h + 1])
                ins.then_inc(free(key), 1)

                act.wait_ge(state_out, 16 * STATE_OUTS * (l + 1))
                normalise(l, 1, [(("mix", 3), l)], sq2)
                act.wait_ge(logit_max, l + 1)
                for b in range(NB):
                    ins = act.activation(rt[:, R_E, b * E:(b + 1) * E], rt[:, R_LOG, b * E:(b + 1) * E], ACT.Exp,
                                         bias=rt[:, R_X, b:b + 1])
                ins.then_inc(logit_exp, 1)
                for i in range(4):
                    b, half = i // 2, i % 2
                    spread((("tok", i), l), htok[:, b, half * 512:(half + 1) * 512])

                base = banks["moe_full", l]

                def pick_out(p, half):
                    act.wait_ge(bank_full[0], 2 * p + (base[0] + half + 1))
                    act.activation(xe[:, 4 * half:4 * half + 4, :], ps[0][:, :].rearrange("p (k c) -> p k c", k=4),
                                   ACT.Copy).then_inc(bank_read[0], 1)

                def silu(p, j):
                    act.wait_ge(bank_full[1], 2 * p + (base[1] + j + 1))
                    act.activation(ex[:, j, :, :], ps[1][:, 0:KF * SLOTS].rearrange("p (f c) -> p f c", f=KF), ACT.Exp,
                                   scale=-1.0).then_inc(silu_exp, 1)

                def pair(p, last=False):
                    silu(p, 0)
                    silu(p, 1)
                    if not last:
                        pick_out(p + 1, 0)
                        pick_out(p + 1, 1)
                    act.wait_ge(bank_full[2], p + (base[2] + 1))
                    act.activation(ye[:, 0:512], ps[2][:, :], ACT.Copy).then_inc(bank_read[2], 1)

                pick_out(0, 0)
                pick_out(0, 1)
                for i in (0, 2):
                    spread((("scat", i), l), scat[:, 2 * i:2 * i + 2, :].rearrange("p a t -> p (a t)"))
                with act.Fori(0, PAIRS - 1) as p:
                    pair(p)
                pair(PAIRS - 1, last=True)
                with act.If(overflow(act, l)):
                    with act.Fori(1, SPILLS * E + 1) as n:
                        act.wait_ge(spill_hidden[l], n)
                        act.activation(sex[:, :, :], ps[2][:, 0:KF * SLOTS].rearrange("p (f c) -> p f c", f=KF), ACT.Exp,
                                       scale=-1.0).then_inc(spill_exp[l], 1)

            for r in (0, 2):
                bank = full(act, ("out", r))
                act.activation(otok[:, r // 2, (r % 2) * 512:(r % 2 + 1) * 512], bank[:, :], ACT.Copy).then_inc(free(("out", r)), 1)

        @block.vector
        def _(dve):
            note, settle, step = stepper(dve, dve_step)
            dve.memset(ones[:, :], 1.0).then_inc(ones_set, 1)
            dve.memset(zeros[:, :], 0.0).then_inc(ones_set, 1)
            dve.memset(eps[:, :], EPS).then_inc(eps_set, 1)
            dve.memset(m0[:, :, :], 0.0).then_inc(m0_clear, 1)
            dve.memset(gpad[:, :, :, :], 0.0)
            dve.wait_ge(cond_exp, 1)
            step(dve.tensor_scalar(conde, conde, 1.0, None, ALU.add))
            step(dve.reciprocal(conde, conde))
            dve.tensor_tensor(condr, condr, conde, ALU.mult).then_inc(cond_silu, 1)
            bank = full(dve, "cond")
            dve.tensor_copy(cT[:, :], bank[:, 0:2 * KD]).then_inc(free("cond"), 1)
            for l in range(DEPTH):
                bank = full(dve, ("rows", l))
                dve.tensor_copy(cols[:, l, :], bank[:, 0:ROWS_L]).then_inc(free(("rows", l)), 1)
            taken(dve, ("rows", DEPTH - 1))

            def modulation_columns(l):
                dve.wait_ge(mod_read, MOD_SLOTS * (l + 1))
                key = ("mod", l)
                dve.tensor_tensor(modc[:, l % 2, :, :], ps[7][:, 0:2 * MODC].rearrange("p (m b) -> p m b", b=NB),
                                  per_col(cols[:, l, 0:MODC], NB), ALU.add).then_inc(free(key), 1)
                taken(dve, key)
                for which, g in enumerate((A_GMIX, A_GFFN)):
                    c = (3 * which + 1) * KD
                    ins = dve.scalar_tensor_tensor(amp[:, l % 2, which, :, :], modc[:, l % 2, c:c + KD, :], 1.0,
                                                   per_col(cols[:, l, g:g + KD], NB), ALU.add, ALU.mult)
                ins.then_inc(mod_ready, 1)

            def normalise(l, which, ready, square):
                taken(dve, *ready)
                dve.tensor_tensor(square[:, 4:8, :], xT[:, 4:8, :], xT[:, 4:8, :], ALU.mult).then_inc(square_v, 1)
                taken(dve, (f"ssq{which + 1}", l))
                step(dve.tensor_tensor(square[:, 0:SPLIT, :], xT[:, 0:SPLIT, :], repeat(rstd[:, :], SPLIT), ALU.mult))
                if l == 0 and which == 0:
                    modulation_columns(0)
                dve.wait_ge(mod_ready, l + 1)
                for k in range(SPLIT):
                    for b in range(NB):
                        ins = dve.tensor_scalar(hT[:, k, b * P:(b + 1) * P], square[:, k, b * P:(b + 1) * P],
                                                amp[:, l % 2, which, k, b:b + 1],
                                                modc[:, l % 2, 3 * KD * which + k, b:b + 1], ALU.mult, ALU.add)
                ins.then_inc(h_ready, 1)

            def residual(l, name, gate):
                for i in range(4):
                    key = ((name, i), l)
                    bank = full(dve, key)
                    for j in range(2):
                        for b in range(NB):
                            x = xT[:, 2 * i + j, b * P:(b + 1) * P]
                            c = j * TOK + b * P
                            ins = dve.scalar_tensor_tensor(x, bank[:, c:c + P], modc[:, l % 2, gate * KD + 2 * i + j, b:b + 1],
                                                           x, ALU.mult, ALU.add)
                    ins.then_inc(free(key), 1)

            for l in range(DEPTH):
                normalise(l, 0, [("x", r) for r in range(4)] if l == 0 else [(("y", 3), l - 1)], sq)

                dve.memset(mv[:, :, :, MD:MD + 1], 1.0)
                if l == 0:
                    dve.wait_ge(small_in, 16 * SMALL_LOADS)
                key = ("gates", l)
                bank = full(dve, key)
                for b in range(NB):
                    ins = dve.tensor_tensor(gpad[:, :, b, :].rearrange("p i (d c) -> p i d c", d=2)[:, :, :, 0:MH],
                                            bank[:, b * NG:(b + 1) * NG].rearrange("p (i d h) -> p i d h", i=2, d=2),
                                            gb[:, l, :].rearrange("p (i d h) -> p i d h", i=2, d=2), ALU.add)
                ins.then_inc(free(key), 1)

                dve.wait_ge(log1p, l + 1)
                step(dve.scalar_tensor_tensor(rows[:, 1, :, :], rows[:, 1, :, :], 0.0, rows[:, 2, :, :], ALU.min, ALU.subtract))
                for b in range(NB):
                    for d in range(2):
                        q, way = slice(32 * d, 32 * d + 32), slice(None, None, 1 - 2 * d)
                        note(dve.tensor_tensor_scan(rows[q, 3, b, way], ones[q, :], rows[q, 1, b, way], 0.0,
                                                         ALU.mult, ALU.add))
                settle()
                step(dve.tensor_tensor(scans[:, :, 1, :], rows[:, 0, :, :], rows[:, 3, :, :], ALU.subtract))
                for b in range(NB):
                    for d in range(2):
                        q, way = slice(32 * d, 32 * d + 32), slice(None, None, 1 - 2 * d)
                        note(dve.tensor_tensor_scan(scans[q, b, 0, way], scans[q, b, 1, way], scans[q, b, 1, way],
                                                         m0[q, l, b:b + 1], ALU.max, ALU.max))
                settle()
                for b in range(NB):
                    dve.tensor_scalar(scans[:, b, 2, :], scans[:, b, 0, :], -1.0, m0[:, l, b:b + 1], ALU.mult, ALU.add)
                    note(dve.scalar_tensor_tensor(scans[:, b, 3, :], rows[:, 3, b, :], -1.0, scans[:, b, 0, :],
                                                       ALU.mult, ALU.subtract))
                    for d in range(2):
                        q, last = slice(32 * d, 32 * d + 32), (P - 1) * (1 - d)
                        dve.tensor_scalar(scans[q, b, 4, :], scans[q, b, 1, :], scans[q, b, 0, last:last + 1], None, ALU.subtract)
                settle()
                for d in range(2):
                    q, last = slice(32 * d, 32 * d + 32), (P - 1) * (1 - d)
                    ins = dve.tensor_scalar(mnew[q, l:l + 1], scans[q, 0, 3, last:last + 1], -1.0, None, ALU.mult)
                ins.then_inc(scan_diff, 1)

                for b in range(NB):
                    key = (("mq", b), l)
                    bank = full(dve, key)
                    dve.tensor_copy(mq[:, b, :], bank[:, :]).then_inc(free(key), 1)
                key = ("scanT", l)
                bank = full(dve, key)
                dve.tensor_copy(qc[:, :, :, :].rearrange("p b q (d h) -> p (b q) d h", d=2),
                                bank[:, :].rearrange("p (n d c) -> p n d c", n=8, d=2)[:, :, :, 0:MH]).then_inc(free(key), 1)
                taken(dve, key)

                def gaps(d):
                    for i in range(2):
                        key = (("mrow", d, i), l)
                        bank = full(dve, key)
                        for j in range(2):
                            for b in range(NB):
                                h, c = 2 * i + j, j * TOK + b * P
                                ins = dve.tensor_scalar(W[:, d, h, b, :], bank[:, c:c + P], qc[:, b, 0, d * MH + h:d * MH + h + 1],
                                                        0.0, ALU.subtract, ALU.max)
                        ins.then_inc(free(key), 1)

                gaps(0)
                for b in range(NB):
                    key = (("akv", b), l)
                    bank = full(dve, key)
                    dve.tensor_copy(qk[:, b, NQ * HD:], bank[:, 0:2 * NKV * HD]).then_inc(free(key), 1)
                gaps(1)
                for b in range(NB):
                    dve.wait_ge(qk_sq, NB * l + b + 1)
                    ins = dve.tensor_reduce(qk_r[:, b, :], qkr[:, b, :].rearrange("p (h d) -> p h d", d=HD), AX_X, ALU.add)
                ins.then_inc(qk_ssq, 1)
                for b in range(NB):
                    key = (("mqT", b), l)
                    if b == 0:
                        dve.wait_ge(qk_rstd, l + 1)
                        for bb in range(NB):
                            heads = qkr[:, bb, :].rearrange("p (h d) -> p h d", d=HD)
                            note(dve.tensor_tensor(heads, qk[:, bb, 0:QW].rearrange("p (h d) -> p h d", d=HD),
                                                        per_col(qk_r[:, bb, :], HD), ALU.mult))
                        settle()
                        for bb in range(NB):
                            heads = qkr[:, bb, :].rearrange("p (h d) -> p h d", d=HD)
                            dve.tensor_tensor(heads[:, 0:NQ, :], heads[:, 0:NQ, :], repeat(gqk[:, l, 0, :], NQ), ALU.mult)
                            ins = dve.tensor_tensor(heads[:, NQ:, :], heads[:, NQ:, :], repeat(gqk[:, l, 1, :], NKV), ALU.mult)
                            if bb == 0:
                                ins.then_inc(qk_ready, 1)
                            else:
                                step(ins)
                        turned = work[:, 0:QW].rearrange("p (h d) -> p h d", d=HD)
                        direct = work[:, QW:2 * QW].rearrange("p (h d) -> p h d", d=HD)
                        dve.tensor_tensor(direct, heads, repeat(cst[:, C_COS:C_COS + HD], NQ + NKV), ALU.mult)
                        for half in range(2):
                            pieces = [a.rearrange("p h (r s i) -> p h r s i", r=2, s=2) for a in (turned, heads)]
                            sin = cst[:, C_SIN:C_SIN + HD].rearrange("p (r s i) -> p r s i", r=2, s=2)
                            ins = dve.tensor_tensor(pieces[0][:, :, :, half, :], pieces[1][:, :, :, 1 - half, :],
                                                    repeat(sin[:, :, half, :], NQ + NKV), ALU.mult)
                        step(ins)
                        dve.tensor_tensor(heads, direct, turned, ALU.add).then_inc(qk_ready, 1)
                    bank = full(dve, key)
                    dve.tensor_copy(mqT[:, b, :, :].rearrange("p h t -> p (h t)"), bank[:, :]).then_inc(free(key), 1)
                dve.wait_ge(decay_ready, 2 * (l + 1))
                for b in range(NB):
                    key = (("ST", b), l)
                    bank = full(dve, key)
                    for d in range(2):
                        ins = dve.tensor_tensor(W[:, d, :, b, :], bank[:, :].rearrange("p (h t) -> p h t", h=MH),
                                                W[:, d, :, b, :], ALU.mult)
                    ins.then_inc(free(key), 1)
                for key, dst in ((("kT1", l), kT1[:, :, :].rearrange("p g t -> p (g t)")),
                                 (("kT0", l), kT0[:, :, :].rearrange("p g t -> p (g t)"))):
                    bank = full(dve, key)
                    dve.tensor_copy(dst, bank[:, 0:dst.shape[1]]).then_inc(free(key), 1)

                def peak(i):
                    key = (f"s1{i}", l) if i < 4 else (f"s0{i - 4}", l)
                    heads = 2 if i < 4 else 4
                    bank = full(dve, key)
                    step(dve.tensor_reduce(att[:, 0, 4 * i:4 * i + heads], bank[:, :].rearrange("p (h k) -> p h k", h=heads),
                                           AX_X, ALU.max))
                    dve.tensor_scalar(att[:, 1, 4 * i:4 * i + heads], att[:, 0, 4 * i:4 * i + heads], -HD ** -0.5, None,
                                      ALU.mult).then_inc(score_max, 1)

                def shares(i):
                    key = (f"s1{i}", l) if i < 4 else (f"s0{i - 4}", l)
                    heads = 2 if i < 4 else 4
                    taken(dve, key)
                    step(dve.reciprocal(att[:, 0, 4 * i:4 * i + heads], att[:, 3, 4 * i:4 * i + heads]))
                    p = prob[:, i * 512:(i + 1) * 512].rearrange("p (h k) -> p h k", h=heads)
                    dve.tensor_tensor(p, p, per_col(att[:, 0, 4 * i:4 * i + heads], 512 // heads), ALU.mult).then_inc(prob_ready, 1)

                peak(0)
                for i in range(6):
                    if i < 5:
                        peak(i + 1)
                    shares(i)
                for key, dst in ((("p11", l), pT1[:, 1, :, :, :].rearrange("p j k t -> p (j k t)")),
                                 (("p13", l), pT1[:, 3, :, :, :].rearrange("p j k t -> p (j k t)")),
                                 (("p01", l), pT0[:, 1, :, :].rearrange("p j t -> p (j t)"))):
                    bank = full(dve, key)
                    dve.tensor_copy(dst, bank[:, :]).then_inc(free(key), 1)
                key = ("o0", l)
                bank = full(dve, key)
                dve.tensor_copy(cat[:, 0:4, 0:P], bank[:, :].rearrange("p (k t) -> p k t", k=4)).then_inc(free(key), 1)
                dve.wait_ge(layer_in, 16 * LAYER_LOADS * (l + 1))
                dve.tensor_copy(C0[:, :, MD:MD + 1], cols[:, l, A_N0:ROWS_L].unsqueeze(2)).then_inc(c0_ready, 1)
                taken(dve, (("mo", 0), l), (("mo", 1), l))
                step(dve.tensor_scalar(og[:, :, :], og[:, :, :], 1.0, None, ALU.add))
                step(dve.reciprocal(og[:, :, :], og[:, :, :]))

                def heads_out(b):
                    den = num[:, b, :, :, MD]
                    step(dve.scalar_tensor_tensor(dn[:, b, :, :], den, -1.0, den, ALU.mult, ALU.max))
                    step(dve.tensor_tensor(dn[:, b, :, :], dn[:, b, :, :], qc[:, b, 2, :].rearrange("p (d h) -> p h d", d=2), ALU.max))
                    step(dve.reciprocal(dn[:, b, :, :], dn[:, b, :, :]))
                    both = num[:, b, :, :, 0:MD].rearrange("p h d e -> p (h d) e")
                    step(dve.tensor_tensor(both, both, per_col(dn[:, b, :, :].rearrange("p h d -> p (h d)"), MD), ALU.mult))
                    step(dve.tensor_tensor(mqT[:, b, :, :], num[:, b, :, 0, 0:MD], num[:, b, :, 1, 0:MD], ALU.add))
                    step(dve.tensor_tensor(num[:, b, :, 0, 0:MD], mqT[:, b, :, :], mqT[:, b, :, :], ALU.mult))
                    dve.tensor_reduce(hr[:, b, :], num[:, b, :, 0, 0:MD], AX_X, ALU.add).then_inc(head_ssq, 1)

                def heads_gated(b):
                    dve.wait_ge(head_rstd, NB * l + b + 1)
                    step(dve.tensor_tensor(mqT[:, b, :, :], mqT[:, b, :, :], per_col(hr[:, b, :], MD), ALU.mult))
                    o = og[:, b, :].rearrange("p (h e) -> p h e", h=MH)
                    dve.tensor_tensor(o, o, mqT[:, b, :, :], ALU.mult).then_inc(ml_ready, 1)

                for h in range(MH):
                    key = (("num", 0, h), l)
                    bank = full(dve, key)
                    dve.tensor_copy(num[:, 0, h, :, :].rearrange("p d e -> p (d e)"), bank[:, 0:2 * (MD + 1)]).then_inc(free(key), 1)
                for h in range(MH):
                    key = (("num", 1, h), l)
                    taken(dve, (("inter", h), l))
                    bank = full(dve, key)
                    dve.tensor_tensor(num[:, 1, h, :, :].rearrange("p d e -> p (d e)"), bank[:, 0:2 * (MD + 1)],
                                      inter_s[:, h % 2, :, :].rearrange("p d e -> p (d e)"), ALU.add).then_inc(free(key), 1)
                taken(dve, (("num", 0, MH - 1), l))
                heads_out(0)
                taken(dve, (("num", 1, MH - 1), l))
                heads_out(1)
                taken(dve, (("C", MH - 1), l))
                dve.tensor_copy(ncol[:, :], Cn[:, :, MD]).then_inc(n_ready, 1)
                heads_gated(0)
                heads_gated(1)
                key = ("nT", l)
                bank = full(dve, key)
                dve.tensor_copy(nst[:, :], bank[0:8, 0:P]).then_inc(free(key), 1)
                key = (("mlT", 1), l)
                bank = full(dve, key)
                for h in range(MH):
                    ins = dve.tensor_scalar(cat[:, MH + h, P:2 * P], bank[:, h * P:(h + 1) * P],
                                            cols[:, l, A_GMH + h:A_GMH + h + 1], None, ALU.mult)
                ins.then_inc(free(key), 1)
                residual(l, "mix", 2)
                if l + 1 < DEPTH:
                    modulation_columns(l + 1)

                dve.wait_ge(state_out, 16 * STATE_OUTS * (l + 1))
                normalise(l, 1, [(("mix", 3), l)], sq2)

                def r(i, lo=0, hi=2 * E):
                    return rt[:, i, lo:hi]

                def beb(i):
                    return r(i).rearrange("p (b e) -> p b e", b=NB)

                key = ("router", l)
                bank = full(dve, key)
                dve.tensor_copy(r(R_LOG), bank[:, 0:2 * E]).then_inc(free(key), 1)
                taken(dve, key)
                step(dve.tensor_reduce(r(R_X, 2, 4), beb(R_LOG), AX_X, ALU.max))
                dve.tensor_scalar(r(R_X, 0, 2), r(R_X, 2, 4), -1.0, None, ALU.mult).then_inc(logit_max, 1)
                dve.wait_ge(logit_exp, l + 1)
                step(dve.tensor_reduce(r(R_X, 4, 6), beb(R_E), AX_X, ALU.add))
                step(dve.reciprocal(r(R_X, 4, 6), r(R_X, 4, 6)))
                step(dve.tensor_tensor(beb(R_E), beb(R_E), per_col(r(R_X, 4, 6), E), ALU.mult))
                step(dve.tensor_tensor(beb(R_SEL), beb(R_E), repeat(brt[:, :], NB), ALU.add))

                def ranks(dst, src, n):
                    v = src.rearrange("p (n i) -> p n i", i=4)
                    other = v.unsqueeze(2).broadcast_to([P, n, 4, 4])
                    mine = v.unsqueeze(3).broadcast_to([P, n, 4, 4])
                    tie = cst[:, C_TIE:C_TIE + 16].rearrange("p (i j) -> p i j", i=4)
                    dve.tensor_tensor(cmpa[:, 0:n], other, mine, ALU.is_gt)
                    step(dve.tensor_tensor(cmpb[:, 0:n], other, mine, ALU.is_equal))
                    step(dve.tensor_tensor(cmpb[:, 0:n], cmpb[:, 0:n], repeat(tie, n), ALU.mult))
                    step(dve.tensor_tensor(cmpa[:, 0:n], cmpa[:, 0:n], cmpb[:, 0:n], ALU.add))
                    step(dve.tensor_reduce(dst.rearrange("p (n i) -> p n i", i=4), cmpa[:, 0:n], AX_X, ALU.add))

                ranks(r(R_T), r(R_SEL), 8)
                step(dve.tensor_scalar(r(R_IN2), r(R_T), 1.5, None, ALU.is_lt))
                step(dve.tensor_tensor(r(R_W), r(R_SEL), r(R_IN2), ALU.mult))
                step(dve.tensor_reduce(r(R_GS, 0, 8), r(R_W).rearrange("p (n i) -> p n i", i=4), AX_X, ALU.add))
                ranks(r(R_GS, 8, 16), r(R_GS, 0, 8), 2)
                step(dve.tensor_scalar(r(R_GS, 16, 24), r(R_GS, 8, 16), 0.5, None, ALU.is_lt))
                dve.tensor_tensor(r(R_MASK).rearrange("p (n i) -> p n i", i=4), r(R_IN2).rearrange("p (n i) -> p n i", i=4),
                                  per_col(r(R_GS, 16, 24), 4), ALU.mult).then_inc(mask_ready, 1)
                dve.wait_ge(mask_ready, l + 1)
                step(dve.tensor_tensor(r(R_W), r(R_E), r(R_MASK), ALU.mult))
                step(dve.tensor_reduce(r(R_X, 6, 8), beb(R_W), AX_X, ALU.add))
                step(dve.reciprocal(r(R_X, 6, 8), r(R_X, 6, 8)))
                dve.tensor_tensor(beb(R_G), beb(R_W), per_col(r(R_X, 6, 8), E), ALU.mult).then_inc(gates_ready, 1)
                key = ("pos", l)
                bank = full(dve, key)
                step(dve.scalar_tensor_tensor(r(R_POS), bank[:, 0:2 * E], 1.0, r(R_MASK), ALU.add, ALU.mult))
                note(dve.tensor_scalar(r(R_POS), r(R_POS), -1.0, None, ALU.add))
                step(dve.tensor_reduce(r(R_X, 8, 9), bank[:, 2 * E:3 * E], AX_X, ALU.max))
                dve.tensor_copy(count_i[:, l:l + 1], r(R_X, 8, 9)).then_inc(free(key), 1)
                for b in range(NB):
                    ins = dve.tensor_tensor(pick[:, b, :, :], repeat(cst[:, C_IOTA:C_IOTA + SLOTS], E),
                                            per_col(r(R_POS, b * E, (b + 1) * E), SLOTS), ALU.is_equal)
                ins.then_inc(pick_ready, 1)
                for i in (1, 3):
                    key = (("scat", i), l)
                    bank = full(dve, key)
                    dve.tensor_copy(scat[:, 2 * i:2 * i + 2, :].rearrange("p a t -> p (a t)"), bank[:, :]).then_inc(free(key), 1)

                base = banks["moe_full", l]

                def pair(p):
                    for j in range(2):
                        n = 3 * (2 * PAIRS * l + j)
                        e = ex[:, j, :, :]
                        gate = ps[1][:, 0:KF * SLOTS].rearrange("p (f c) -> p f c", f=KF)
                        up = ps[1][:, KF * SLOTS:].rearrange("p (f c) -> p f c", f=KF)
                        dve.wait_ge(silu_exp, 2 * p + (2 * PAIRS * l + j + 1))
                        dve.tensor_scalar(e, e, 1.0, None, ALU.add).then_inc(silu_step, 1)
                        dve.wait_ge(silu_step, 6 * p + (n + 1))
                        dve.reciprocal(e, e).then_inc(silu_step, 1)
                        dve.wait_ge(silu_step, 6 * p + (n + 2))
                        dve.tensor_tensor(e, gate, e, ALU.mult).then_inc(silu_step, 1)
                        dve.wait_ge(silu_step, 6 * p + (n + 3))
                        dve.tensor_tensor(hid[:, j, :, :], up, e, ALU.mult).then_inc(bank_read[1], 1)
                    dve.wait_ge(bank_full[3], p + (base[3] + 1))
                    dve.tensor_copy(ye[:, 512:1024], ps[3][:, :]).then_inc(bank_read[3], 1)

                with dve.Fori(0, PAIRS) as p:
                    pair(p)

                def spill(e, c):
                    n = SPILLS * e + c + 1
                    dve.wait_ge(spill_turn[l], n)
                    for b in range(NB):
                        one = rt[:, R_POS, bass.ds(e + b * E, 1)].broadcast_to([P, SLOTS])
                        ins = dve.tensor_tensor(spick[:, b, :], cst[:, bass.ds(c * SLOTS + (C_IOTA + SLOTS), SLOTS)], one,
                                                ALU.is_equal)
                    ins.then_inc(spill_silu[l], 1)
                    m = 6 * SPILLS * e + 6 * c
                    dve.wait_ge(spill_silu[l], m + 1)
                    for b in range(NB):
                        one = rt[:, R_G, bass.ds(e + b * E, 1)].broadcast_to([P, SLOTS])
                        ins = dve.tensor_tensor(sgate[:, b, :], spick[:, b, :], one, ALU.mult)
                    ins.then_inc(spill_pick[l], 1)
                    dve.wait_ge(spill_gathered[l], n)
                    dve.tensor_copy(xe[:, 0:4, :].rearrange("p k c -> p (k c)"), ps[0][:, :]).then_inc(spill_silu[l], 1)
                    dve.tensor_copy(sscat[:, :], ps[1][0:SLOTS, 0:TOK]).then_inc(spill_in[l], 1)
                    gate = ps[2][:, 0:KF * SLOTS].rearrange("p (f c) -> p f c", f=KF)
                    up = ps[2][:, KF * SLOTS:].rearrange("p (f c) -> p f c", f=KF)
                    dve.wait_ge(spill_exp[l], n)
                    dve.tensor_scalar(sex[:, :, :], sex[:, :, :], 1.0, None, ALU.add).then_inc(spill_silu[l], 1)
                    dve.wait_ge(spill_silu[l], m + 3)
                    dve.reciprocal(sex[:, :, :], sex[:, :, :]).then_inc(spill_silu[l], 1)
                    dve.wait_ge(spill_silu[l], m + 4)
                    dve.tensor_tensor(sex[:, :, :], gate, sex[:, :, :], ALU.mult).then_inc(spill_silu[l], 1)
                    dve.wait_ge(spill_silu[l], m + 5)
                    dve.tensor_tensor(shid[:, :, :], up, sex[:, :, :], ALU.mult).then_inc(spill_act[l], 1)
                    dve.wait_ge(spill_down[l], n)
                    dve.tensor_copy(ye[0:SLOTS, 0:512], ps[0][0:SLOTS, :]).then_inc(spill_silu[l], 1)
                    dve.tensor_copy(ye[0:SLOTS, 512:1024], ps[1][0:SLOTS, :]).then_inc(spill_back[l], 1)

                with dve.If(overflow(dve, l)):
                    dve.sem_inc(spill_turn[l], 1)
                    with dve.Fori(0, E) as e:
                        with dve.Fori(0, SPILLS) as c:
                            spill(e, c)
                residual(l, "y", 5)

            for r in (1, 3):
                bank = full(dve, ("out", r))
                dve.tensor_copy(otok[:, r // 2, (r % 2) * 512:(r % 2 + 1) * 512], bank[:, :]).then_inc(free(("out", r)), 1)

        @block.gpsimd
        def _(pool):
            def layer_loads(l):
                pool.dma_start(C0[:, :, 0:MD], t["state_C"][0, l].rearrange("a h d e -> d (a h) e")).then_inc(layer_in, 16)
                pool.dma_start(ck[:, :], t["cache_k"][0, l].rearrange("s g d -> s (g d)")).then_inc(layer_in, 16)
                pool.dma_start(cv[:, :], t["cache_v"][0, l].rearrange("s g d -> s (g d)")).then_inc(layer_in, 16)

            layer_loads(0)
            for l in range(DEPTH):
                def share_of_norm(which, square):
                    taken(pool, (f"ssq{which + 1}", l))
                    pool.tensor_tensor(square[:, SPLIT:KD, :], xT[:, SPLIT:KD, :], repeat(rstd[:, :], KD - SPLIT),
                                       ALU.mult).then_inc(normed_g, 1)

                share_of_norm(0, sq)
                pool.wait_ge(const_in, 16)
                for b in range(NB):
                    taken(pool, (("aq", b), l), (("akv", b), l))
                    pool.tensor_tensor(qkr[:, b, :], qk[:, b, 0:QW], qk[:, b, 0:QW], ALU.mult).then_inc(qk_sq, 1)
                for d in range(2):
                    pool.wait_ge(decay_exp, 2 * l + d + 1)
                    w = W[:, d, :, :, :].rearrange("p h b t -> p (h b) t")
                    pool.tensor_tensor(w, w, repeat(keep[:, d, :], MH * NB), ALU.mult).then_inc(decay_ready, 1)
                pool.wait_ge(qk_ready, NB * l + 1)
                pool.dma_start(t["new_cache_k"][0, l].rearrange("s g d -> s (g d)"), qkr[:, 0, NQ * HD:]).then_inc(kv_out, 16)
                pool.dma_start(t["new_cache_v"][0, l].rearrange("s g d -> s (g d)"), qk[:, 0, QW:]).then_inc(kv_out, 16)
                full(pool, (("mqT", 1), l))
                taken(pool, ("scanT", l), (("mk", 0), l))
                for d in range(2):
                    pool.tensor_tensor(kw[:, d, :, :], mk[:, 0, :].rearrange("p (h e) -> p h e", h=MH),
                                       per_col(qc[:, 0, 3, d * MH:(d + 1) * MH], MD), ALU.mult).then_inc(kw_ready, 1)
                for d in range(2):
                    pool.dma_start(t["new_state_m"][0, l, d, :].unsqueeze(1), mnew[32 * d:32 * d + MH, l:l + 1]).then_inc(state_out, 16)
                if l + 1 < DEPTH:
                    full(pool, ("o1", l))
                    full(pool, (("inter", MH - 1), l))
                    layer_loads(l + 1)
                taken(pool, (("C", MH - 1), l))
                pool.dma_start(t["new_state_C"][0, l].rearrange("a h d e -> d (a h) e"), Cn[:, :, 0:MD]).then_inc(state_out, 16)
                taken(pool, ("nT", l))
                pool.dma_start(t["new_state_n"][0, l].rearrange("a h c -> (a h) c"), nst[:, :]).then_inc(state_out, 16)
                pool.wait_ge(state_out, 16 * STATE_OUTS * (l + 1))
                share_of_norm(1, sq2)
                pool.wait_ge(gates_ready, l + 1)
                pool.wait_ge(pick_ready, l + 1)
                for b in range(NB):
                    ins = pool.tensor_tensor(gpick[:, b, :, :], pick[:, b, :, :],
                                             per_col(rt[:, R_G, b * E:(b + 1) * E], SLOTS), ALU.mult)
                ins.then_inc(gpick_ready, 1)
            pool.wait_ge(kv_out, 32 * DEPTH)


_INS = ["x_prompt", "x_sample", "c", "cache_k", "cache_v", "state_C", "state_n", "state_m", "c_ctx", "w_mod",
        "b_mod", "g_mix", "g_ffn", "w_in", "b_igate", "b_fgate", "g_q", "g_k", "g_mh", "w_out", "w_router",
        "b_router", "w_e_gate", "w_e_up", "w_e_down"]
_OUTS = [("y_prompt", (1, P, D)), ("y_sample", (1, P, D)), ("new_cache_k", (1, DEPTH, P, NKV, HD)),
         ("new_cache_v", (1, DEPTH, P, NKV, HD)), ("new_state_C", (1, DEPTH, 2, MH, MD, MD)),
         ("new_state_n", (1, DEPTH, 2, MH, MD)), ("new_state_m", (1, DEPTH, 2, MH))]


def kernel(**inputs):
    import concourse.bacc as bacc
    from concourse.bass_utils import run_bass_kernel_spmd

    nc = bacc.Bacc("TRN2", target_bir_lowering=False, num_devices=1)
    arrays = {f"in_{name}": np.ascontiguousarray(inputs[name]) for name in _INS}
    arrays["in_constants"] = shape_constants()
    t = {}
    for name, a in arrays.items():
        t[name[3:]] = nc.dram_tensor(name, a.shape, mybir.dt.from_np(a.dtype), kind="ExternalInput").ap()
    for name, shape in _OUTS:
        t[name] = nc.dram_tensor(f"out_{name}", shape, F32, kind="ExternalOutput").ap()
    build(nc, t)
    r = run_bass_kernel_spmd(nc, [arrays], core_ids=[0])
    return tuple(r.results[0][f"out_{name}"] for name, _ in _OUTS)
```
